# Optimizing a Trainium2 kernel written in Bass

```python
import math
import jax, jax.numpy as jnp
from jax import lax
import numpy as np

D_MODEL = 4096
BATCH = 1
SEQ = 256
DEPTH = 1

CHUNK = 64
Q_BLOCK = 128
HEAD_DIM = 128
ATTN_WIDTH = D_MODEL // 2
ATTN_HEADS = ATTN_WIDTH // HEAD_DIM
RNN_WIDTH = D_MODEL // 2
RNN_BLOCKS = 16
RNN_BLOCK_DIM = RNN_WIDTH // RNN_BLOCKS
CONV_W = 4
RG_C = 8.0
N_BRANCH = 2
EPS = 1e-6
IN_SPLITS = (ATTN_WIDTH, ATTN_WIDTH, ATTN_WIDTH, ATTN_WIDTH, ATTN_HEADS, RNN_WIDTH, RNN_WIDTH)
IN_COLS = sum(IN_SPLITS)

kernel_name = "hybrid_fox_rglru_gated_merge"

def _rms(xf, eps=EPS):
    return xf * lax.rsqrt(jnp.mean(jnp.square(xf), axis=-1, keepdims=True) + eps)

def _split_cols(p):
    idx = np.cumsum(IN_SPLITS)[:-1].tolist()
    return jnp.split(p, idx, axis=-1)

def _forgetting_attention(q, k, v, log_f):
    B, H, S, Dh = q.shape
    n_blocks = S // Q_BLOCK
    scale = 1.0 / math.sqrt(Dh)
    F = jnp.cumsum(log_f, axis=-1)
    k_pos = jnp.arange(S)

    def block(i):
        start = i * Q_BLOCK
        q_blk = lax.dynamic_slice_in_dim(q, start, Q_BLOCK, axis=2)
        F_q = lax.dynamic_slice_in_dim(F, start, Q_BLOCK, axis=2)
        s = jnp.einsum('bhqd,bhkd->bhqk', q_blk, k) * scale
        s = s + (F_q[..., :, None] - F[..., None, :])
        q_pos = start + jnp.arange(Q_BLOCK)
        mask = q_pos[:, None] >= k_pos[None, :]
        s = jnp.where(mask, s, jnp.float32(-1e30))
        p = jax.nn.softmax(s, axis=-1)
        return jnp.einsum('bhqk,bhkd->bhqd', p, v)

    out = lax.map(block, jnp.arange(n_blocks))
    out = jnp.transpose(out, (1, 2, 0, 3, 4)).reshape(B, H, S, Dh)
    return out

def _causal_depthwise_conv(x, w, b):
    S = x.shape[1]
    xp = jnp.pad(x, ((0, 0), (CONV_W - 1, 0), (0, 0)))
    out = b
    for tap in range(CONV_W):
        out = out + xp[:, tap:tap + S, :] * w[tap]
    return out

def _rg_lru(xr, w_rg_a, b_rg_a, w_rg_x, b_rg_x, lru_lambda):
    B, S, W = xr.shape
    xb = xr.reshape(B, S, RNN_BLOCKS, RNN_BLOCK_DIM)
    r = jax.nn.sigmoid(jnp.einsum('bsnd,nde->bsne', xb, w_rg_a).reshape(B, S, W) + b_rg_a)
    i = jax.nn.sigmoid(jnp.einsum('bsnd,nde->bsne', xb, w_rg_x).reshape(B, S, W) + b_rg_x)
    log_a = -RG_C * r * jax.nn.softplus(-lru_lambda)
    a = jnp.exp(log_a)
    mult = jnp.sqrt(-jnp.expm1(2.0 * log_a))
    bx = mult * (i * xr)

    def combine(left, right):
        a_l, b_l = left
        a_r, b_r = right
        return a_l * a_r, a_r * b_l + b_r

    _, h = lax.associative_scan(combine, (a, bx), axis=1)
    return h

def setup_inputs(seed: int = 0) -> dict:
    key = jax.random.key(seed)
    ks = jax.random.split(key, 24)
    D = D_MODEL
    f32 = jnp.float32
    nrm = lambda k, shape, s: jax.random.normal(k, shape, f32) * s
    x = nrm(ks[0], (BATCH, SEQ, D), 1.0)
    c = nrm(ks[1], (BATCH, D), 1.0)
    w_ada = nrm(ks[2], (D, 3 * D), 0.5 * D ** -0.5)
    b_ada = nrm(ks[3], (3 * D,), 0.02)
    norm_w = 1.0 + nrm(ks[4], (D,), 0.02)
    w_in = nrm(ks[5], (D, IN_COLS), D ** -0.5)
    b_f = 3.0 + nrm(ks[6], (ATTN_HEADS,), 0.5)
    q_norm_w = 1.0 + nrm(ks[7], (HEAD_DIM,), 0.02)
    k_norm_w = 1.0 + nrm(ks[8], (HEAD_DIM,), 0.02)
    conv_w = nrm(ks[9], (CONV_W, RNN_WIDTH), CONV_W ** -0.5)
    conv_b = nrm(ks[10], (RNN_WIDTH,), 0.02)
    w_rg_a = nrm(ks[11], (RNN_BLOCKS, RNN_BLOCK_DIM, RNN_BLOCK_DIM), RNN_BLOCK_DIM ** -0.5)
    b_rg_a = nrm(ks[12], (RNN_WIDTH,), 0.02)
    w_rg_x = nrm(ks[13], (RNN_BLOCKS, RNN_BLOCK_DIM, RNN_BLOCK_DIM), RNN_BLOCK_DIM ** -0.5)
    b_rg_x = nrm(ks[14], (RNN_WIDTH,), 0.02)
    a_base = jax.random.uniform(ks[15], (RNN_WIDTH,), f32, 0.9, 0.999)
    sig_l = a_base ** (1.0 / RG_C)
    lru_lambda = jnp.log(sig_l) - jnp.log1p(-sig_l)
    w_br_attn = nrm(ks[16], (ATTN_WIDTH, D), ATTN_WIDTH ** -0.5)
    w_br_rnn = nrm(ks[17], (RNN_WIDTH, D), RNN_WIDTH ** -0.5)
    w_gate = nrm(ks[18], (D, N_BRANCH * D), D ** -0.5)
    b_gate = nrm(ks[19], (N_BRANCH * D,), 0.02)
    w_out = nrm(ks[20], (D, D), D ** -0.5)
    return {"x": x, "c": c, "w_ada": w_ada, "b_ada": b_ada, "norm_w": norm_w,
            "w_in": w_in, "b_f": b_f, "q_norm_w": q_norm_w, "k_norm_w": k_norm_w,
            "conv_w": conv_w, "conv_b": conv_b, "w_rg_a": w_rg_a, "b_rg_a": b_rg_a,
            "w_rg_x": w_rg_x, "b_rg_x": b_rg_x, "lru_lambda": lru_lambda,
            "w_br_attn": w_br_attn, "w_br_rnn": w_br_rnn, "w_gate": w_gate,
            "b_gate": b_gate, "w_out": w_out}

def reference(x, c, w_ada, b_ada, norm_w, w_in, b_f, q_norm_w, k_norm_w, conv_w, conv_b,
              w_rg_a, b_rg_a, w_rg_x, b_rg_x, lru_lambda, w_br_attn, w_br_rnn, w_gate,
              b_gate, w_out):
    dt = x.dtype
    f32 = jnp.float32
    B, S, D = x.shape
    mod = jnp.dot(jax.nn.silu(c.astype(f32)), w_ada.astype(f32)) + b_ada.astype(f32)
    shift, scale, gate_res = jnp.split(mod, 3, axis=-1)

    for _layer in range(DEPTH):
        h = _rms(x.astype(f32)) * norm_w.astype(f32)
        h = (h * (1.0 + scale[:, None, :]) + shift[:, None, :]).astype(dt)

        proj = jnp.einsum('bsd,de->bse', h, w_in)
        q, k, v, z_a, f_logit, x_r, z_r = _split_cols(proj)

        def heads(t):
            return t.reshape(B, S, ATTN_HEADS, HEAD_DIM).transpose(0, 2, 1, 3).astype(f32)
        qh = _rms(heads(q)) * q_norm_w.astype(f32)
        kh = _rms(heads(k)) * k_norm_w.astype(f32)
        vh = heads(v)
        log_f = jax.nn.log_sigmoid(f_logit.astype(f32) + b_f.astype(f32))
        log_f = jnp.transpose(log_f, (0, 2, 1))
        att = _forgetting_attention(qh, kh, vh, log_f)
        att = att.transpose(0, 2, 1, 3).reshape(B, S, ATTN_WIDTH)
        y_a = (att * jax.nn.silu(z_a.astype(f32))).astype(dt)
        y_a = jnp.einsum('bsw,wd->bsd', y_a, w_br_attn)

        xc = _causal_depthwise_conv(x_r.astype(f32), conv_w.astype(f32), conv_b.astype(f32))
        hr = _rg_lru(xc, w_rg_a.astype(f32), b_rg_a.astype(f32), w_rg_x.astype(f32),
                     b_rg_x.astype(f32), lru_lambda.astype(f32))
        y_r = (hr * jax.nn.silu(z_r.astype(f32))).astype(dt)
        y_r = jnp.einsum('bsw,wd->bsd', y_r, w_br_rnn)

        g = jax.nn.sigmoid(jnp.einsum('bsd,de->bse', h, w_gate).astype(f32) + b_gate.astype(f32))
        g_a, g_r = jnp.split(g, N_BRANCH, axis=-1)
        merged = (g_a * y_a.astype(f32) + g_r * y_r.astype(f32)).astype(dt)
        out = jnp.einsum('bsd,de->bse', merged, w_out)
        x = (x.astype(f32) + gate_res[:, None, :] * out.astype(f32)).astype(dt)
    return x


_drawn_inputs = setup_inputs


def setup_inputs(seed=0):
    import zlib

    import numpy as np

    out = dict(_drawn_inputs(seed))
    spreads = {}
    factors = {'b_ada': 3.884,
     'norm_w': 8.0,
     'b_f': 6.715,
     'q_norm_w': 8.0,
     'k_norm_w': 8.0,
     'conv_b': 6.569,
     'w_rg_a': 2.871,
     'b_rg_a': 64.0,
     'b_rg_x': 41.322,
     'b_gate': 21.846}
    for name, (base, spread) in spreads.items():
        noise = np.random.default_rng([zlib.crc32(name.encode()), seed]).standard_normal(out[name].shape)
        drawn = base * np.exp(spread * noise) if base else spread * noise
        out[name] = __import__('jax').numpy.asarray(drawn.astype(out[name].dtype))
    for name, factor in factors.items():
        out[name] = (out[name] * factor).astype(out[name].dtype)
    return out
```

```python
from contextlib import ExitStack

import concourse.bass as bass
from concourse import mybir

F32 = mybir.dt.float32
F32R = mybir.dt.float32r
ALU = mybir.AluOpType
ACT = mybir.ActivationFunctionType
AX = mybir.AxisListType
ds = bass.ds

P = 128
D = 4096
SEQ = 256
NT = SEQ // P
KT = D // P
HEADS = 16
WIDTH = HEADS * P
BLOCKS = WIDTH // P
TAPS = 4
EPS = 1e-6
CW = 512
UK = 2
UROWS = UK * P
BPJ = CW // P
LAND = 4
PARTS = 2
ACCS = 2
WAVES = 4
HALVES = 2
JPB = 10
WU = D // WAVES // UROWS
GU = D // UROWS
RU = WIDTH // UROWS
CH = D // CW
XR_COL = 4 * WIDTH + HEADS
ZR_COL = XR_COL + WIDTH

BODY = JPB * WU
N_HEADS0 = WAVES * HALVES * BODY
N_MA0 = N_HEADS0 + 4 * GU
N_MR0 = N_MA0 + CH * (GU + RU)
N_OUT0 = N_MR0 + CH * (GU + RU)
J_HEADS0 = WAVES * HALVES * JPB
J_MA0 = J_HEADS0 + 4
J_MR0 = J_MA0 + 2 * CH
J_OUT0 = J_MR0 + 2 * CH

K_BLK, V_BLK, ZA_BLK, XR_BLK, ZR_BLK = 16, 32, 48, 64, 80
ADA_T = D // P

LOG1P_TERMS = 7
FREE = 1


class Steps:

    def __init__(self, eng, sem):
        self.eng, self.sem, self.base, self.n = eng, sem, 0, 0
        self.last = None

    def did(self, instruction, sem=None, value=None):
        if sem is None:
            self.n += 1
            instruction.then_inc(self.sem, 1)
            self.last = (self.sem, self.base + self.n)
        else:
            instruction.then_inc(sem, 1)
            self.last = (sem, value)

    def sync(self):
        if self.last is not None:
            self.eng.wait_ge(*self.last)


def heads_plan():
    plan = {}
    for i in range(8):
        at = 1 + 3 * i
        for step, off in (("turn", 0), ("score", 1), ("probs", 3), ("value", 4), ("y", 6)):
            plan.setdefault(at + off, []).append((step, i))
    return plan


def build(nc, x, c, w_ada, b_ada, norm_w, w_in, b_f, q_norm_w, k_norm_w, conv_w, conv_b,
          w_rg_a, b_rg_a, w_rg_x, b_rg_x, lru_lambda, w_br_attn, w_br_rnn, w_gate, b_gate,
          w_out, y):
    ctx = ExitStack()
    with ctx:
        base = (nc.sbuf_base + 31) // 32 * 32
        top = [base]

        def region(nbytes):
            at = top[0]
            top[0] += (nbytes + 31) // 32 * 32
            assert top[0] <= nc.sbuf_usable_end
            return at

        def at(name, shape, dt, offset):
            return nc.alloc_sbuf_tensor_at(name, shape, dt, offset=offset)

        def psum(name, shape):
            return ctx.enter_context(nc.psum_tensor(name, shape, F32))

        def sem(name):
            return ctx.enter_context(nc.semaphore(name))

        KB = 1024
        r_hi, r_lo = region(32 * KB), region(32 * KB)
        r_store = region(96 * KB)
        r_land, r_whi, r_wlo = region(16 * KB), region(8 * KB), region(8 * KB)
        r_scr = region(12 * KB)

        h_hi = at("h_hi", [P, KT, NT, P], F32R, r_hi)
        h_lo = at("h_lo", [P, KT, NT, P], F32R, r_lo)
        store = at("store", [P, 96, NT, P], F32, r_store)
        blk = lambda b: r_store + b * KB
        x_full = at("x_full", [P, NT, D], F32, blk(0))
        ada_land = at("ada_land", [P, LAND, 2, CW], F32, blk(ZR_BLK))
        wf = at("wf", [P, KT, HEADS], F32, blk(ZR_BLK))
        wf_parts = at("wf_parts", [P, KT, 2, 3, HEADS], F32R, blk(ZR_BLK + 2))
        za_sig = at("za_sig", [P, BPJ, NT, P], F32, blk(ZR_BLK + 8))
        ya_hi = at("ya_hi", [P, HEADS, NT, P], F32R, blk(0))
        ya_lo = at("ya_lo", [P, HEADS, NT, P], F32R, blk(K_BLK))
        yr_hi = at("yr_hi", [P, BLOCKS, NT, P], F32R, blk(XR_BLK))
        yr_lo = at("yr_lo", [P, BLOCKS, NT, P], F32R, blk(ZR_BLK))
        merged = at("merged", [P, CH, NT, CW], F32, blk(V_BLK))
        res_gate = at("res_gate", [P, CH, CW], F32, blk(0))
        res_land = at("res_land", [P, LAND, 2, CW], F32, blk(K_BLK))
        x_out = at("x_out", [P, 2, NT, CW], F32, blk(XR_BLK))

        land = at("land", [P, LAND, UK, CW], F32, r_land)
        w_hi = at("w_hi", [P, PARTS, UK, CW], F32R, r_whi)
        w_lo = at("w_lo", [P, PARTS, UK, CW], F32R, r_wlo)

        ident = at("ident", [P, P], F32, region(512))
        ones = at("ones", [P, P], F32, region(512))
        mask = at("mask", [P, P], F32, region(512))
        cols = at("cols", [P, P], F32, region(512))
        prm = at("prm", [P, P], F32, region(512))
        cvec = at("cvec", [P, ADA_T], F32, region(128))
        sp = at("sp", [P, 2, BLOCKS], F32, region(128))
        modc = at("modc", [P, 2, BPJ], F32, region(32))
        rstd = at("rstd", [P, NT], F32, region(32))
        bf_col = at("bf_col", [P, 1], F32, region(32))
        mx = at("mx", [P, NT], F32, region(32))
        den = at("den", [P, NT], F32, region(32))
        rden = at("rden", [P, NT], F32, region(32))
        rqk = at("rqk", [P, 2 * HEADS, NT], F32, region(256))

        K = KB
        acc = at("acc", [P, 2, CW], F32, r_scr)
        xs = at("xs", [P, NT, CW], F32, r_scr + 4 * K)
        hmod = at("hmod", [P, BPJ, NT, P], F32, r_scr + 8 * K)
        raw1 = at("raw1", [P, P], F32, r_scr + 8 * K)
        raw2 = at("raw2", [P, P], F32, r_scr + 8 * K + 512)
        spt = at("spt", [P, 6, BLOCKS], F32, r_scr + 9 * K)
        csig = at("csig", [P, ADA_T], F32, r_scr + 10 * K)

        qn = at("qn", [P, 2, NT, P], F32, r_scr)
        qkt = at("qkt", [P, 2, NT * P], F32, r_scr + 2 * K)
        lt = at("lt", [48, 6, SEQ], F32, r_scr)
        pr = at("pr", [P, 3, P], F32, r_scr + 4 * K)
        prt = at("prt", [P, 3, P], F32, r_scr + 5 * K + 512)
        yt = at("yt", [P, NT, P], F32, r_scr + 7 * K)
        fl = at("fl", [48, SEQ], F32, r_scr + 8 * K)
        fr = at("fr", [48, SEQ], F32, r_scr + 9 * K)
        ff = at("ff", [48, SEQ], F32, r_scr + 10 * K)
        junk = at("junk", [P, P], F32, r_scr + 11 * K + 512)

        gate = at("gate", [P, NT, CW], F32, r_scr)
        xz = at("xz", [P, 2, NT, P], F32, r_scr + 4 * K)
        th = at("th", [P, SEQ], F32, r_scr + 4 * K)
        av = at("av", [P, SEQ], F32, r_scr + 5 * K)
        xc = at("xc", [P, SEQ], F32, r_scr + 6 * K)
        ri = at("ri", [P, 2, SEQ], F32, r_scr + 7 * K)
        wrg = at("wrg", [P, 2, P], F32, r_scr + 9 * K)
        bx = at("bx", [P, SEQ], F32, r_scr + 10 * K)
        hh = at("hh", [P, SEQ], F32, r_scr + 11 * K)
        racc = at("racc", [P, CW], F32, r_scr + 4 * K)
        rbias = at("rbias", [P, CW], F32, r_scr + 6 * K)
        otmp = at("otmp", [P, NT, CW], F32, r_scr)

        ps_acc = psum("ps_acc", [P, ACCS, NT, CW])
        ps_t = psum("ps_t", [P, 2, NT, NT, P])
        ps_c = psum("ps_c", [P, 512])
        ps_d = psum("ps_d", [P, 512])
        bank4 = ps_t[:, 0].rearrange("p a b c -> p (a b c)")
        bank5 = ps_t[:, 1].rearrange("p a b c -> p (a b c)")
        tq = bank4.rearrange("p (a b) -> p a b", a=4)
        ps_s = bank5[:, 0:3 * P].rearrange("p (a b) -> p a b", a=3)
        ps_p = ps_c[:, 0:3 * P].rearrange("p (a b) -> p a b", a=3)
        ps_o = ps_d[:, 0:2 * P].rearrange("p (a b) -> p a b", a=2)
        ps_y = ps_d[:, 2 * P:4 * P].rearrange("p (a b) -> p a b", a=2)
        rt = tq
        ps_g = bank5.rearrange("p (a b) -> p a b", a=2)

        landed = [sem(f"landed{i}") for i in range(LAND)]
        ada_landed = [sem(f"ada_landed{i}") for i in range(LAND)]
        hi_rdy, hi_used = sem("hi_rdy"), sem("hi_used")
        split_done, unit_done, acc_free = sem("split_done"), sem("unit_done"), sem("acc_free")
        ada_used, res_used = sem("ada_used"), sem("res_used")
        dve_step, act_step = sem("dve_step"), sem("act_step")
        small_in, x_in, xs_in, wf_in = sem("small_in"), sem("x_in"), sem("xs_in"), sem("wf_in")
        consts, cleared, cols_t = sem("consts"), sem("cleared"), sem("cols_t")
        ss_rdy, ms_rdy, rt_rdy, rstd_rdy = sem("ss_rdy"), sem("ms_rdy"), sem("rt_rdy"), sem("rstd_rdy")
        sp_in, sp_e = sem("sp_in"), sem("sp_e")
        c_in, c_sig = sem("c_in"), sem("c_sig")
        xs_rdy, xs_t, colsum, mod_rdy = sem("xs_rdy"), sem("xs_t"), sem("colsum"), sem("mod_rdy")
        h_mod, h_rnd, h_rdy = sem("h_mod"), sem("h_rnd"), sem("h_rdy")
        wf_hi, wf_rdy, f_done = sem("wf_hi"), sem("wf_rdy"), sem("f_done")
        lf_in, lf_e = sem("lf_in"), sem("lf_e")
        stat, stat_ms, stat_sq, rqk_rdy = sem("stat"), sem("stat_ms"), sem("stat_sq"), sem("rqk_rdy")
        za_s, za_m, zr_s = sem("za_s"), sem("za_m"), sem("zr_s")
        qn_rdy, lr_rdy, turned, qkt_rdy = sem("qn_rdy"), sem("lr_rdy"), sem("turned"), sem("qkt_rdy")
        scored, mx_rdy, pr_rdy, pr_t, prt_rdy = (sem("scored"), sem("mx_rdy"), sem("pr_rdy"),
                                                 sem("pr_t"), sem("prt_rdy"))
        valued, y_rdy, y_t, ya_h, ya_rdy = (sem("valued"), sem("y_rdy"), sem("y_t"), sem("ya_h"),
                                            sem("ya_rdy"))
        bias_in, gate_sum, gate_rdy, gate_used = (sem("bias_in"), sem("gate_sum"), sem("gate_rdy"),
                                                  sem("gate_used"))
        wrg_in, xz_rdy, xz_t, tap0, xc_rdy, rg_done = (sem("wrg_in"), sem("xz_rdy"), sem("xz_t"),
                                                       sem("tap0"), sem("xc_rdy"), sem("rg_done"))
        ri_rdy, m2_rdy, mult_rdy, hh_rdy, yr_h, yr_rdy = (sem("ri_rdy"), sem("m2_rdy"),
                                                          sem("mult_rdy"), sem("hh_rdy"),
                                                          sem("yr_h"), sem("yr_rdy"))
        racc_rdy, rsum, rg_rdy, rbias_in = sem("racc_rdy"), sem("rsum"), sem("rg_rdy"), sem("rbias_in")
        res_landed = [sem(f"res_landed{i}") for i in range(LAND)]
        mt_t, mt_h, mt_rdy = sem("mt_t"), sem("mt_h"), sem("mt_rdy")
        xo_in = [sem(f"xo_in{i}") for i in range(2)]
        out_rdy = sem("out_rdy")
        stored = [sem(f"stored{i}") for i in range(2)]

        rows = lambda w: w.rearrange("(k p) n -> p k n", p=P)
        w_in_v, w_gate_v, w_out_v = rows(w_in), rows(w_gate), rows(w_out)
        w_ba_v, w_br_v = rows(w_br_attn), rows(w_br_rnn)
        ada_v = w_ada.rearrange("(p t) (s n) -> p t s n", t=ADA_T, s=3)
        x_v = x.rearrange("b (t p) n -> p (b t) n", p=P)
        y_v = y.rearrange("b (t p) n -> p (b t) n", p=P)

        block = ctx.enter_context(nc.Block())

        heads_at = heads_plan()
        BLK_AT = lambda i: 1 + 12 * i

        wf_thrice = wf[:].unsqueeze(2).to_broadcast([P, KT, 3, HEADS])

        def ada_tile(u):
            return u - u // 9 if u < ADA_T * 9 // 8 and u % 9 != 8 else None

        def landed_at(n0, u):
            return (n0 + (u - u % LAND)) * (16 // LAND) + 16

        def mt_ps(k):
            return ps_t[:].rearrange("p a b c d -> p (a b) c d")

        @block.gpsimd
        def _(pool):
            pool.memset(ident[:], 0.0).then_inc(consts, 1)
            pool.memset(mask[:], 0.0).then_inc(consts, 1)
            pool.memset(ones[:], 1.0).then_inc(consts, 1)
            pool.wait_ge(consts, 3)
            pool.affine_select(out=ident[:], in_=ident[:], compare_op=ALU.not_equal, fill=1.0,
                               base=0, pattern=[[-1, P]], channel_multiplier=1).then_inc(consts, 1)
            pool.affine_select(out=mask[:], in_=mask[:], compare_op=ALU.is_ge, fill=-1e30,
                               base=0, pattern=[[-1, P]], channel_multiplier=1).then_inc(consts, 1)

        @block.sync
        def _(sp_):
            def load(n0, u, src):
                sp_.wait_ge(split_done, n0 + u + 1)
                sp_.dma_start(land[:, u % LAND], src).then_inc(landed[u % LAND], 16)

            def load_ada(hg, t):
                sp_.wait_ge(ada_used, 32 * hg + t + 1)
                sp_.dma_start(ada_land[:, t % LAND],
                              ada_v[:, t, 0:2, ds(hg * CW, CW)]).then_inc(ada_landed[t % LAND], 16)

            def load_xs(hg):
                if not isinstance(hg, int) or hg > 0:
                    sp_.wait_ge(xs_t, hg)
                sp_.dma_start(xs[:], x_v[:, :, ds(hg * CW, CW)]).then_inc(xs_in, 16)

            one = lambda v: v.rearrange("(a b) -> a b", b=P)
            sp_.dma_start(cvec[:], c.rearrange("b (p t) -> (b p) t", t=ADA_T)).then_inc(c_in, 16)
            for t in range(LAND):
                load_ada(0, t)
            sp_.dma_start(raw1[0:64, :], one(b_ada)[0:64, :]).then_inc(small_in, 16)
            sp_.dma_start(raw1[64:96, :], one(norm_w)).then_inc(small_in, 16)
            sp_.dma_start(raw1[96:97, :], one(q_norm_w)).then_inc(small_in, 16)
            sp_.dma_start(raw1[97:98, :], one(k_norm_w)).then_inc(small_in, 16)
            sp_.dma_start(raw2[0:64, :], conv_w.rearrange("t (a b) -> (t a) b", b=P)).then_inc(small_in, 16)
            sp_.dma_start(raw2[64:80, :], one(conv_b)).then_inc(small_in, 16)
            sp_.dma_start(raw2[80:96, :], one(b_rg_a)).then_inc(small_in, 16)
            sp_.dma_start(raw2[96:112, :], one(b_rg_x)).then_inc(small_in, 16)
            sp_.dma_start(raw2[112:128, :], one(lru_lambda)).then_inc(small_in, 16)
            sp_.wait_ge(cleared, 1)
            sp_.dma_start(bf_col[0:16, :], b_f.rearrange("(a b) -> a b", b=1)).then_inc(small_in, 16)
            sp_.dma_start(bf_col[32:48, :], b_f.rearrange("(a b) -> a b", b=1)).then_inc(small_in, 16)
            for t in range(NT):
                sp_.dma_start(x_full[:, t, :], x_v[:, t, :]).then_inc(x_in, 16)
            for hg in range(2):
                load_xs(hg)
                for t in range(ADA_T):
                    if hg > 0 or t >= LAND:
                        load_ada(hg, t)

            def wave_body(g, b, ada):
                n0 = (g * 2 + b) * BODY
                hg = g * 2 + b + 2
                for i in range(JPB):
                    col = (b * 8 + i) * CW if i < 8 else (b * 2 + i - 8) * CW + XR_COL
                    for u in range(WU):
                        load(n0, i * WU + u, w_in_v[:, ds(g * WU * UK + u * UK, UK), ds(col, CW)])
                        if ada and ada_tile(i * WU + u) is not None:
                            load_ada(hg, ada_tile(i * WU + u))
                    if ada and i == 0:
                        load_xs(hg)

            with sp_.Fori(0, WAVES - 1) as g:
                with sp_.Fori(0, HALVES) as b:
                    wave_body(g, b, True)
            sp_.wait_ge(ada_used, 256 + LAND)
            sp_.dma_start(wf[:], w_in_v[:, :, 4 * WIDTH:XR_COL]).then_inc(wf_in, 16)
            with sp_.Fori(0, HALVES) as b:
                wave_body(WAVES - 1, b, False)

            with sp_.Fori(0, 2) as it:
                for i in range(2):
                    for u in range(GU):
                        load(N_HEADS0 + it * 2 * GU, i * GU + u,
                             w_in_v[:, u * UK:(u + 1) * UK, ds((it * 2 + i) * CW + ZR_COL, CW)])

            b_gate_v = b_gate.rearrange("(a n) -> a n", a=1)
            b_ada_v = b_ada.rearrange("(a n) -> a n", a=1)

            def merge(cc, r):
                n0 = (N_MR0 if r else N_MA0) + cc * (GU + RU)
                col = sp_.snap(cc * CW)
                for u in range(GU + RU):
                    if u < GU:
                        load(n0, u, w_gate_v[:, u * UK:(u + 1) * UK, ds(col + r * D, CW)])
                    else:
                        src = w_br_v if r else w_ba_v
                        v = u - GU
                        load(n0, u, src[:, v * UK:(v + 1) * UK,
                                        ds((cc + 1) * CW - CW if r and v == 0 else col, CW)])
                    if u == 6:
                        sp_.wait_ge(ya_rdy, HEADS)
                        sp_.wait_ge(gate_used, (CH + 2 * cc if r else cc) + FREE)
                        for t in range(NT):
                            sp_.dma_start(gate[:, t], b_gate_v[:, ds(cc * CW + r * D, CW)]
                                          .to_broadcast([P, CW])).then_inc(bias_in, 16)
                    if not r and u in (3, 15):
                        i = u // 12
                        sp_.wait_ge(ya_rdy, HEADS)
                        n = cc * 2 + i
                        sp_.wait_ge(rg_done, n + FREE)
                        sp_.dma_start(wrg[:, 0], w_rg_a[n]).then_inc(wrg_in, 16)
                        sp_.dma_start(wrg[:, 1], w_rg_x[n]).then_inc(wrg_in, 16)
                    if r and 2 <= u < 22 and (u - 2) % 5 != 4:
                        v = u - 2 - (u - 2) // 5
                        sp_.wait_ge(unit_done, N_MR0 + PARTS)
                        sp_.wait_ge(res_used, cc * 16 + v + 1)
                        sp_.dma_start(res_land[:, v % LAND], ada_v[:, 2 * v:2 * v + 2, 2, ds(cc * CW, CW)]
                                      ).then_inc(res_landed[v % LAND], 16)
                    if r and u == 8:
                        sp_.wait_ge(yr_rdy, BLOCKS)
                        sp_.wait_ge(rg_rdy, cc + FREE)
                        sp_.dma_start(rbias[:], b_ada_v[:, ds(2 * D + cc * CW, CW)].to_broadcast([P, CW])
                                      ).then_inc(rbias_in, 16)

            with sp_.Fori(0, CH) as cc:
                merge(cc, 0)
            with sp_.Fori(0, CH) as cc:
                merge(cc, 1)

            def out_job(cc, i, first):
                n0 = N_OUT0 + cc * GU
                for u in range(GU):
                    load(n0, i * GU + u, w_out_v[:, u * UK:(u + 1) * UK, ds((cc + i) * CW, CW)])
                    if u == 6 and first:
                        sp_.wait_ge(unit_done, N_OUT0 + PARTS)
                    if u == 8:
                        if not (first and i < 2):
                            sp_.wait_ge(stored[i % 2], (cc + i) * 8 - i % 2 * 8)
                        sp_.dma_start(x_out[:, i % 2], x_v[:, :, ds((cc + i) * CW, CW)]
                                      ).then_inc(xo_in[i % 2], 16)
                    if u == 10 and not (first and i == 0):
                        sp_.wait_ge(out_rdy, cc + i)
                        sp_.dma_start(y_v[:, :, ds((cc + i - 1) * CW, CW)], x_out[:, (i + 1) % 2]
                                      ).then_inc(stored[(i + 1) % 2], 16)

            out_job(0, 0, True)
            out_job(0, 1, True)
            with sp_.Fori(1, CH // 2) as pair:
                cc = pair * 2
                out_job(cc, 0, False)
                out_job(cc, 1, False)
            sp_.wait_ge(out_rdy, CH)
            sp_.dma_start(y_v[:, :, (CH - 1) * CW:], x_out[:, 1]).then_inc(stored[1], 16)
            sp_.wait_ge(stored[0], 16 * CH // 2)
            sp_.wait_ge(stored[1], 16 * CH // 2)

        @block.scalar
        def _(act):
            st = Steps(act, act_step)

            def hi(n0, u):
                act.wait_ge(landed[u % LAND], landed_at(n0, u))
                act.wait_ge(hi_used, n0 + u + 1)
                if not (isinstance(n0, int) and n0 + u < 2):
                    act.wait_ge(split_done, n0 + u + LAND - PARTS + 1)
                act.activation(w_hi[:, u % PARTS], land[:, u % LAND], ACT.Copy).then_inc(hi_rdy, 1)

            def prep_scale(hg):
                act.wait_ge(xs_in, hg * 16 + 16)
                for t in range(NT):
                    act.activation(xs[:, t], xs[:, t], ACT.Copy, scale=rstd[:, t:t + 1]).then_inc(xs_rdy, 1)

            def prep_mod(hg, kks):
                if kks[0] == 0:
                    act.wait_ge(xs_t, hg + 1)
                    act.wait_ge(mod_rdy, hg + 1)
                    act.wait_ge(h_rdy, hg)
                for kk in kks:
                    act.activation(hmod[:, kk], ps_t[:, kk // 2, kk % 2], ACT.Identity,
                                   bias=modc[:, 0, kk:kk + 1], scale=modc[:, 1, kk:kk + 1]).then_inc(h_mod, 1)

            def prep_round(hg):
                act.wait_ge(h_mod, hg * 4 + 4)
                act.activation(h_hi[:, ds(hg * 4, 4)], hmod[:], ACT.Copy).then_inc(h_rnd, 1)

            act.wait_ge(c_in, 16)
            act.activation(csig[:], cvec[:], ACT.Sigmoid).then_inc(c_sig, 1)
            act.wait_ge(sp_in, 1)
            act.activation(spt[:, 1], spt[:, 0], ACT.Exp, scale=-1.0).then_inc(sp_e, 1)
            act.wait_ge(x_in, 32)
            for t in range(NT):
                act.activation(x_full[:, t], x_full[:, t], ACT.Square, accum_out=mx[:, t:t + 1]
                               ).then_inc(ss_rdy, 1)
            act.wait_ge(ms_rdy, 1)
            act.activation(mx[:], mx[:], ACT.Sqrt).then_inc(rt_rdy, 1)
            act.wait_ge(rstd_rdy, 1)
            for hg in range(2):
                prep_scale(hg)
                prep_mod(hg, range(4))
                prep_round(hg)

            def wave_body(g, b, ada):
                n0 = (g * 2 + b) * BODY
                hg = g * 2 + b + 2
                for i in range(JPB):
                    for u in range(WU):
                        hi(n0, i * WU + u)
                        if ada:
                            if (i, u) == (4, 0):
                                prep_scale(hg)
                            if (i, u) == (9, 3):
                                prep_mod(hg, range(4))
                                prep_round(hg)
                        elif isinstance(b, int):
                            if b == 0 and (i, u) == (0, 1):
                                act.wait_ge(wf_in, 16)
                                act.activation(wf_parts[:, :, 0], wf_thrice, ACT.Copy).then_inc(wf_hi, 1)
                            if b == 0 and (i, u) == (8, 2):
                                act.wait_ge(lf_in, 1)
                                act.activation(lt[:, 1], lt[:, 0], ACT.Exp, scale=-1.0).then_inc(lf_e, 1)
                            if b == 0 and 1 <= i < 9 and u == 3:
                                act.wait_ge(acc_free, n0 // BODY * JPB + i + ACCS)
                                for k in range(BPJ):
                                    for t in range(NT):
                                        if i > 1 or k or t:
                                            act.wait_ge(stat, ((i - 1) * BPJ + k) * NT + t)
                                        blk_no = (i - 1) * BPJ + k
                                        act.activation(junk[:], store[:, blk_no, t], ACT.Square,
                                                       accum_out=rqk[:, blk_no, t:t + 1]).then_inc(stat, 1)
                            if b == 1 and (i, u) == (0, 3):
                                act.wait_ge(stat_ms, 1)
                                act.activation(rqk[:], rqk[:], ACT.Sqrt).then_inc(stat_sq, 1)
                            if b == 1 and 5 <= i < 9 and u == 3:
                                act.wait_ge(acc_free, n0 // BODY * JPB + i + ACCS)
                                if i > 5:
                                    act.wait_ge(za_m, i - 5)
                                act.activation(za_sig[:], store[:, V_BLK + (i - 1) * BPJ:V_BLK + i * BPJ],
                                               ACT.Sigmoid).then_inc(za_s, 1)

            with act.Fori(0, WAVES - 1) as g:
                with act.Fori(0, HALVES) as b:
                    wave_body(g, b, True)
            wave_body(WAVES - 1, 0, False)
            wave_body(WAVES - 1, 1, False)

            def zr_sig(j, par):
                act.wait_ge(unit_done, N_HEADS0 + (j + 1) * GU + PARTS)
                act.activation(store[:, ds(ZR_BLK + j * BPJ, BPJ)].rearrange("p b t d -> p t b d"),
                               ps_acc[:, par].rearrange("p t (b d) -> p t b d", d=P),
                               ACT.Sigmoid).then_inc(zr_s, 1)

            def head_step(step, h):
                if step == "turn":
                    act.wait_ge(turned, h + 1)
                    act.wait_ge(scored, h)
                    act.activation(qkt[:, 0], tq[:, 0:2].rearrange("p a b -> p (a b)"), ACT.Copy,
                                   scale=cols[:, 98:99]).then_inc(qkt_rdy, 1)
                    act.activation(qkt[:, 1], tq[:, 2:4].rearrange("p a b -> p (a b)"), ACT.Copy
                                   ).then_inc(qkt_rdy, 1)
                if step == "score":
                    act.wait_ge(mx_rdy, h + 1)
                    act.wait_ge(pr_t, h)
                    act.activation(pr[:, 0], ps_s[:, 0], ACT.Exp, bias=mx[:, 0:1],
                                   accum_out=den[:, 0:1]).then_inc(pr_rdy, 1)
                    act.activation(pr[:, 1:3], ps_s[:, 1:3], ACT.Exp, bias=mx[:, 1:2],
                                   accum_out=den[:, 1:2]).then_inc(pr_rdy, 1)
                if step == "y":
                    act.wait_ge(y_t, h + 1)
                    act.activation(ya_hi[:, ds(h, 1)].rearrange("p a t d -> p (a t) d"), ps_y,
                                   ACT.Copy).then_inc(ya_h, 1)

            def heads_body(it, first):
                n0 = N_HEADS0 + it * 2 * GU
                for u in range(2 * GU):
                    hi(n0, u)
                    if u == 17 or (u == 1 and not first):
                        zr_sig(it * 2 + (0 if u == 17 else -1), 0 if u == 17 else 1)
                    for step, i in heads_at.get(u - 2, []):
                        head_step(step, it * 8 + i)

            heads_body(0, True)
            heads_body(1, False)

            def rg_step(off, n):
                if off == -1:
                    act.wait_ge(yr_rdy, n)
                    act.activation(xz[:].rearrange("p s t d -> p s (t d)"), xz_src(n), ACT.Copy
                                   ).then_inc(xz_rdy, 1)
                if off == 2:
                    act.wait_ge(xz_t, n + 1)
                    act.activation(xc[:], rt[:, 0:2].rearrange("p a b -> p (a b)"), ACT.Identity,
                                   bias=prm[:, ds(n + 64, 1)], scale=prm[:, ds(n + 48, 1)]).then_inc(tap0, 1)
                if off == 5:
                    act.wait_ge(rg_done, n + 1 + FREE)
                    act.activation(ri[:, 0], ps_g[:, 0], ACT.Sigmoid, bias=prm[:, ds(n + 80, 1)]
                                   ).then_inc(ri_rdy, 1)
                    act.activation(ri[:, 1], ps_g[:, 1], ACT.Sigmoid, bias=prm[:, ds(n + 96, 1)]
                                   ).then_inc(ri_rdy, 1)
                    act.wait_ge(ri_rdy, n * 4 + 1 + FREE)
                    act.activation(th[:], ri[:, 0], ACT.Tanh, scale=sp[:, 0, ds(n, 1)]).then_inc(ri_rdy, 1)
                if off == 6:
                    act.activation(av[:], ri[:, 0], ACT.Exp, scale=sp[:, 1, ds(n, 1)]).then_inc(ri_rdy, 1)
                if off == 8:
                    act.wait_ge(m2_rdy, n + 1)
                    act.activation(bx[:], bx[:], ACT.Sqrt, scale=2.0).then_inc(mult_rdy, 1)
                if off == 10:
                    act.wait_ge(hh_rdy, n + 1 + FREE)
                    act.activation(yr_hi[:, ds(n, 1)].rearrange("p a t d -> p (a t d)"), hh[:], ACT.Copy
                                   ).then_inc(yr_h, 1)

            def xz_src(n):
                pair = store[:, XR_BLK:ZR_BLK + BLOCKS].rearrange("p (s b) t d -> p s b (t d)", s=2)
                return pair[:, :, ds(n, 1), :].rearrange("p s b e -> p (s b) e")

            def merge(cc, r, prev_zr):
                n0 = (N_MR0 if r else N_MA0) + cc * (GU + RU)
                for u in range(GU + RU):
                    hi(n0, u)
                    if prev_zr and u == 1:
                        zr_sig(3, 1)
                    if u == GU + 2:
                        act.wait_ge(gate_sum, cc + r * CH + 1 + FREE)
                        act.activation(gate[:], gate[:], ACT.Sigmoid).then_inc(gate_rdy, 1)
                    if not r:
                        for i in range(2):
                            rg_step(u - BLK_AT(i), cc * 2 + i)

            merge(0, 0, True)
            with act.Fori(1, CH) as cc:
                merge(cc, 0, False)
            with act.Fori(0, CH - 1) as cc:
                merge(cc, 1, False)

            def mt_round(k):
                act.wait_ge(mt_t, k + 1)
                act.activation(h_hi[:, k * BPJ:(k + 1) * BPJ], mt_ps(k), ACT.Copy).then_inc(mt_h, 1)

            n0 = N_MR0 + (CH - 1) * (GU + RU)
            for u in range(GU + RU):
                hi(n0, u)
                if u == GU + 2:
                    act.wait_ge(gate_sum, 2 * CH + FREE)
                    act.activation(gate[:], gate[:], ACT.Sigmoid).then_inc(gate_rdy, 1)
                if u >= GU + 2:
                    mt_round(u - GU - 2)
            for u in range(2 * GU):
                hi(N_OUT0, u)
                if u == 0:
                    mt_round(CH - 2)
                if u == 5:
                    mt_round(CH - 1)
            with act.Fori(1, CH // 2) as pair:
                cc = pair * 2
                for u in range(2 * GU):
                    hi(N_OUT0 + cc * GU, u)

        @block.vector
        def _(dve):
            st = Steps(dve, dve_step)

            def lo(n0, u):
                dve.wait_ge(hi_rdy, n0 + u + 1)
                dve.wait_ge(unit_done, n0 + u + 1)
                dve.tensor_tensor(w_lo[:, u % PARTS], land[:, u % LAND], w_hi[:, u % PARTS].bitcast(F32),
                                  ALU.subtract).then_inc(split_done, 1)

            def ada(hg, t):
                dve.wait_ge(ada_landed[t % LAND], hg * 128 + (t // LAND + 1) * 16)
                flat = acc[:].rearrange("p s n -> p (s n)")
                src = ada_land[:, t % LAND].rearrange("p s n -> p (s n)")
                if t == 0:
                    dve.wait_ge(colsum, hg)
                    dve.wait_ge(ada_used, hg * 32 + LAND)
                    ins = dve.tensor_scalar(flat, src, cvec[:, t:t + 1], None, ALU.mult)
                else:
                    dve.wait_ge(ada_used, hg * 32 + t + LAND)
                    ins = dve.scalar_tensor_tensor(flat, src, cvec[:, t:t + 1], flat, ALU.mult, ALU.add)
                ins.then_inc(ada_used, 1)

            def prep_cols(hg):
                dve.wait_ge(colsum, hg + 1)
                dve.wait_ge(h_mod, hg * 4)
                bias = cols[:, 0:2 * KT].rearrange("p (s k) -> p s k", s=2)
                dve.tensor_tensor(modc[:], ps_c[:, 0:2 * BPJ].rearrange("p (s k) -> p s k", s=2),
                                  bias[:, :, ds(hg * BPJ, BPJ)], ALU.add).then_inc(dve_step, 1)
                st.n += 1
                dve.wait_ge(dve_step, st.base + st.n)
                dve.scalar_tensor_tensor(modc[:, 1], modc[:, 1], 1.0, cols[:, ds(hg * BPJ + 2 * KT, BPJ)],
                                         ALU.add, ALU.mult).then_inc(mod_rdy, 1)

            def prep_lo(hg):
                dve.wait_ge(h_rnd, hg + 1)
                dve.tensor_tensor(h_lo[:, ds(hg * 4, 4)], hmod[:], h_hi[:, ds(hg * 4, 4)].bitcast(F32),
                                  ALU.subtract).then_inc(h_rdy, 1)

            def log1p_exp(t):
                def op(f, *a):
                    st.did(f(*a))
                    st.sync()
                op(dve.tensor_scalar, t(2), t(1), 2.0, None, ALU.add)
                op(dve.reciprocal, t(2), t(2))
                op(dve.tensor_tensor, t(3), t(1), t(2), ALU.mult)
                op(dve.tensor_tensor, t(4), t(3), t(3), ALU.mult)
                op(dve.tensor_scalar, t(2), t(4), 1.0 / (2 * LOG1P_TERMS + 1), None, ALU.mult)
                for k in range(LOG1P_TERMS - 1, 0, -1):
                    op(dve.scalar_tensor_tensor, t(2), t(2), 1.0 / (2 * k + 1), t(4), ALU.add, ALU.mult)
                op(dve.scalar_tensor_tensor, t(2), t(2), 1.0, t(3), ALU.add, ALU.mult)

            dve.memset(bf_col[:], 0.0).then_inc(cleared, 1)
            free = ((ada_used, LAND), (split_done, LAND), (hi_used, PARTS), (unit_done, PARTS), (acc_free, ACCS),
                    (res_used, LAND), (rg_done, FREE), (gate_used, FREE), (rg_rdy, FREE), (gate_sum, FREE),
                    (hh_rdy, FREE), (ri_rdy, FREE))
            for k, (what, slots) in enumerate(free):
                dve.memset(junk[:, k * 8:(k + 1) * 8], 0.0).then_inc(what, slots)
            dve.wait_ge(c_in, 16)
            dve.wait_ge(c_sig, 1)
            st.did(dve.tensor_tensor(cvec[:], cvec[:], csig[:], ALU.mult))
            st.sync()
            dve.memset(store[:, ZR_BLK - BPJ:ZR_BLK], 0.0).then_inc(cleared, 1)
            dve.wait_ge(cleared, 2)

            def params():
                dve.wait_ge(small_in, 176)
                dve.wait_ge(cols_t, 1)
                st.did(dve.tensor_copy(cols[:, 0:98], bank4[:, 0:98]))
                dve.wait_ge(cols_t, 2)
                st.did(dve.tensor_copy(prm[:], bank5[:, 0:P]))
                st.sync()
                st.did(dve.scalar_tensor_tensor(cols[:, 98:99], cols[:, 96:97], float(P) ** -0.5,
                                                cols[:, 97:98], ALU.mult, ALU.mult))
                st.did(dve.scalar_tensor_tensor(spt[:, 0], prm[:, 112:128], -1.0, prm[:, 112:128], ALU.mult,
                                                ALU.max), sp_in, 1)

            def softplus():
                dve.wait_ge(sp_e, 1)
                log1p_exp(lambda k: spt[:, k])
                st.did(dve.tensor_scalar(spt[:, 5], prm[:, 112:128], -1.0, 0.0, ALU.mult, ALU.max))
                st.sync()
                st.did(dve.scalar_tensor_tensor(spt[:, 5], spt[:, 2], 2.0, spt[:, 5], ALU.mult, ALU.add))
                st.sync()
                st.did(dve.tensor_scalar(sp[:, 0], spt[:, 5], 8.0, None, ALU.mult))
                st.did(dve.tensor_scalar(sp[:, 1], spt[:, 5], -8.0, None, ALU.mult))

            for hg in range(2):
                for t in range(ADA_T):
                    ada(hg, t)
                    if hg == 0 and t == 7:
                        params()
                    if hg == 0 and t == 14:
                        softplus()
                    if hg == 0 and t == 24:
                        dve.wait_ge(ss_rdy, NT)
                        dve.tensor_scalar(mx[:], mx[:], 1.0 / D, EPS, ALU.mult, ALU.add).then_inc(ms_rdy, 1)
                    if hg == 0 and t == 26:
                        dve.wait_ge(rt_rdy, 1)
                        dve.reciprocal(rstd[:], mx[:]).then_inc(rstd_rdy, 1)
                prep_cols(hg)
                prep_lo(hg)

            def job_view(p):
                return ps_acc[:, p].rearrange("p t (b d) -> p b t d", d=P)

            def add_partial(job, n_end, par, first_block, copy=False):
                dve.wait_ge(unit_done, n_end + PARTS)
                dve.wait_ge(acc_free, job + ACCS)
                part = store[:, ds(first_block, BPJ)]
                if copy:
                    dve.tensor_copy(part, job_view(par)).then_inc(acc_free, 1)
                else:
                    dve.tensor_tensor(part, job_view(par), part, ALU.add).then_inc(acc_free, 1)

            def wave_body(g, b, with_ada, first):
                n0 = (g * 2 + b) * BODY
                j0 = (g * 2 + b) * JPB
                hg = g * 2 + b + 2
                for i in range(JPB):
                    for u in range(WU):
                        lo(n0, i * WU + u)
                        if u == 1:
                            if i > 0:
                                k = i - 1
                                blk_no = b * 32 + k * BPJ if k < 8 else b * 8 + XR_BLK + (k - 8) * BPJ
                                add_partial(j0 + k, n0 + i * WU, k % 2, blk_no, isinstance(g, int) and g == 0)
                            elif not first:
                                add_partial(j0 - 1, n0, 1, b * -8 + (XR_BLK + BPJ + 8),
                                            isinstance(g, int) and g == 0)
                        if with_ada and ada_tile(i * WU + u) is not None:
                            ada(hg, ada_tile(i * WU + u))
                        if with_ada and (i, u) == (9, 2):
                            prep_cols(hg)
                        if with_ada and (i, u) == (9, 3):
                            prep_lo(hg)
                        if not with_ada and b == 0 and (i, u) == (0, 2):
                            dve.wait_ge(wf_hi, 1)
                            dve.tensor_tensor(wf_parts[:, :, 1], wf_thrice, wf_parts[:, :, 0].bitcast(F32),
                                              ALU.subtract).then_inc(wf_rdy, 1)
                        if not with_ada and b == 0:
                            if (i, u) == (7, 2):
                                f_abs()
                            if (i, u) == (9, 2):
                                f_scan()
                        if not with_ada and b == 1 and (i, u) == (0, 2):
                            dve.wait_ge(stat, 2 * HEADS * NT)
                            dve.tensor_scalar(rqk[:], rqk[:], 1.0 / P, EPS, ALU.mult, ALU.add).then_inc(stat_ms, 1)
                        if not with_ada and b == 1 and (i, u) == (1, 2):
                            dve.wait_ge(stat_sq, 1)
                            st.did(dve.reciprocal(rqk[:], rqk[:]))
                        if not with_ada and b == 1 and 6 <= i < 10 and u == 0:
                            za_mul(i - 6)

            def f_abs():
                dve.wait_ge(small_in, 176)
                for t_, ones_at in ((fl, 32), (fr, 0)):
                    st.did(dve.memset(t_[:], 0.0))
                    st.sync()
                    st.did(dve.memset(t_[ones_at:ones_at + 16, :], 1.0))
                dve.wait_ge(f_done, 1)
                st.did(dve.tensor_scalar(lt[:, 5], bank4[0:48, 0:SEQ], bf_col[0:48, 0:1], None, ALU.add))
                st.sync()
                st.did(dve.scalar_tensor_tensor(lt[:, 0], lt[:, 5], -1.0, lt[:, 5], ALU.mult, ALU.max), lf_in, 1)

            def f_scan():
                dve.wait_ge(lf_e, 1)
                log1p_exp(lambda k: lt[:, k])
                st.did(dve.tensor_scalar(lt[:, 5], lt[:, 5], 0.0, None, ALU.min))
                st.sync()
                st.did(dve.scalar_tensor_tensor(lt[:, 5], lt[:, 2], -2.0, lt[:, 5], ALU.mult, ALU.add))
                st.did(dve.memset(lt[:, 4], 1.0))
                st.sync()
                st.did(dve.tensor_tensor_scan(ff[:], lt[:, 4], lt[:, 5], 0.0, ALU.mult, ALU.add))
                st.sync()

            def za_mul(k):
                dve.wait_ge(za_s, k + 1)
                part = store[:, ZA_BLK + k * BPJ:ZA_BLK + (k + 1) * BPJ]
                dve.tensor_tensor(part, part, za_sig[:], ALU.mult).then_inc(za_m, 1)

            steps0 = st.n
            wave_body(0, 0, True, True)
            wave_body(0, 1, True, False)
            assert st.n == steps0 + 2
            with dve.Fori(1, WAVES - 1) as g:
                with dve.Fori(0, HALVES) as b:
                    st.n, st.base = 0, g * 2 + b + steps0
                    wave_body(g, b, True, False)
            st.n, st.base = steps0 + 2 * (WAVES - 1), 0
            wave_body(WAVES - 1, 0, False, False)
            wave_body(WAVES - 1, 1, False, False)

            def head_pre(h, first):
                if not first:
                    dve.wait_ge(turned, h)
                qk = store[:, 0:2 * HEADS].rearrange("p (s b) t d -> p s b t d", s=2)
                r = rqk[:].rearrange("p (s b) t -> p s b t", s=2)
                for s in range(2):
                    ins = dve.tensor_tensor(qn[:, s], qk[:, s, ds(h, 1)].rearrange("p b t d -> p (b t) d"),
                                            r[:, s, ds(h, 1)].rearrange("p b t -> p (b t)")
                                            .unsqueeze(2).to_broadcast([P, NT, P]), ALU.mult)
                    ins.then_inc(qn_rdy, 1)

            def head_f(h):
                dve.wait_ge(scored, h)
                dve.tensor_scalar(fl[0:16, :], ff[0:16, :], ident[0:16, ds(h, 1)], None, ALU.mult
                                  ).then_inc(lr_rdy, 1)
                dve.tensor_scalar(fr[32:48, :], ff[32:48, :], ident[32:48, ds(h + 32, 1)], -1.0, ALU.mult,
                                  ALU.mult).then_inc(lr_rdy, 1)

            def head_step(step, h):
                if step == "score":
                    dve.wait_ge(scored, h + 1)
                    st.did(dve.tensor_tensor(ps_s[:, 0:3:2], ps_s[:, 0:3:2],
                                             mask[:].unsqueeze(1).to_broadcast([P, 2, P]), ALU.add))
                    st.sync()
                    dve.wait_ge(pr_rdy, h * 2)
                    st.did(dve.tensor_reduce(mx[:, 0:1], ps_s[:, 0], AX.X, ALU.max))
                    st.did(dve.tensor_reduce(mx[:, 1:2], ps_s[:, 1:3], AX.XY, ALU.max))
                    st.sync()
                    st.did(dve.tensor_scalar(mx[:], mx[:], -1.0, None, ALU.mult), mx_rdy, h + 1)
                if step == "probs":
                    dve.wait_ge(pr_t, h + 1)
                    dve.wait_ge(valued, h)
                    dve.tensor_copy(prt[:], ps_p).then_inc(prt_rdy, 1)
                    st.did(dve.reciprocal(rden[:], den[:]))
                if step == "value":
                    st.sync()
                    dve.wait_ge(valued, h + 1)
                    dve.wait_ge(y_t, h)
                    for t in range(NT):
                        dve.scalar_tensor_tensor(yt[:, t], ps_o[:, t], rden[:, t:t + 1],
                                                 store[:, ds(ZA_BLK + h, 1), t].rearrange("p a d -> p (a d)"),
                                                 ALU.mult, ALU.mult).then_inc(y_rdy, 1)
                if step == "y":
                    dve.wait_ge(ya_h, h + 1)
                    dve.tensor_tensor(ya_lo[:, ds(h, 1)].rearrange("p a t d -> p (a t) d"), ps_y,
                                      ya_hi[:, ds(h, 1)].rearrange("p a t d -> p (a t) d").bitcast(F32),
                                      ALU.subtract).then_inc(ya_rdy, 1)

            def zr_mul(j, par):
                dve.wait_ge(zr_s, j + 1)
                dve.wait_ge(acc_free, J_HEADS0 + j + ACCS)
                part = store[:, ds(ZR_BLK + j * BPJ, BPJ)]
                dve.tensor_tensor(part, job_view(par), part, ALU.mult).then_inc(acc_free, 1)

            def heads_body(it, first):
                n0 = N_HEADS0 + it * 2 * GU
                for u in range(2 * GU):
                    lo(n0, u)
                    if first and u == 1:
                        add_partial(J_HEADS0 - 1, N_HEADS0, 1, XR_BLK + 3 * BPJ)
                    if u == 17 or (u == 1 and not first):
                        zr_mul(it * 2 + (0 if u == 17 else -1), 0 if u == 17 else 1)
                    for step, i in heads_at.get(u + 1, []):
                        if step == "turn":
                            head_pre(it * 8 + i, first and i == 0)
                    for step, i in heads_at.get(u, []):
                        if step == "turn":
                            head_f(it * 8 + i)
                    for step, i in heads_at.get(u - 2, []):
                        head_step(step, it * 8 + i)

            heads_body(0, True)
            heads_body(1, False)

            def rg_step(off, n):
                if off == 2:
                    dve.wait_ge(tap0, n + 1)
                    for back in range(1, TAPS):
                        st.did(dve.scalar_tensor_tensor(
                            xc[:, back:], rt[:, 0:2].rearrange("p a b -> p (a b)")[:, :SEQ - back],
                            prm[:, ds(n + 16 * (TAPS - 1 - back), 1)], xc[:, back:], ALU.mult, ALU.add),
                            *((xc_rdy, n + 1) if back == TAPS - 1 else ()))
                        st.sync()
                if off == 5:
                    dve.wait_ge(ri_rdy, n * 4 + 3 + FREE)
                    st.did(dve.tensor_scalar(bx[:], th[:], 1.0, None, ALU.add))
                    st.sync()
                    st.did(dve.reciprocal(bx[:], bx[:]))
                if off == 6:
                    st.sync()
                    dve.scalar_tensor_tensor(bx[:], th[:], 1.3e-35, bx[:], ALU.max, ALU.mult
                                             ).then_inc(m2_rdy, 1)
                if off == 8:
                    dve.wait_ge(mult_rdy, n + 1)
                    dve.wait_ge(ri_rdy, n * 4 + 4 + FREE)
                    for o, a, bb, op in ((bx, bx, ri[:, 1], 0), (bx, bx, xc[:], 0)):
                        st.did(dve.tensor_tensor(o[:], a[:], bb, ALU.mult))
                        st.sync()
                    st.did(dve.tensor_tensor_scan(hh[:], av[:], bx[:], 0.0, ALU.mult, ALU.add))
                    st.sync()
                    st.did(dve.tensor_tensor(hh[:], rt[:, 2:4].rearrange("p a b -> p (a b)"), hh[:],
                                             ALU.mult), hh_rdy, n + 1 + FREE)
                if off == 10:
                    dve.wait_ge(yr_h, n + 1)
                    dve.tensor_tensor(yr_lo[:, ds(n, 1)].rearrange("p a t d -> p (a t d)"), hh[:],
                                      yr_hi[:, ds(n, 1)].rearrange("p a t d -> p (a t d)").bitcast(F32),
                                      ALU.subtract).then_inc(yr_rdy, 1)

            def gate_add(cc, r):
                n0 = (N_MR0 if r else N_MA0) + cc * (GU + RU)
                dve.wait_ge(unit_done, n0 + GU + PARTS)
                dve.wait_ge(bias_in, (cc + r * CH) * 32 + 32)
                st.did(dve.tensor_tensor(gate[:], ps_acc[:, 0], gate[:], ALU.add), gate_sum,
                       cc + r * CH + 1 + FREE)

            def merge_in(cc, r):
                n0 = (N_MR0 if r else N_MA0) + cc * (GU + RU)
                dve.wait_ge(unit_done, n0 + GU + RU + PARTS)
                dve.wait_ge(gate_rdy, cc + r * CH + 1)
                part = merged[:, ds(cc, 1)].rearrange("p a t n -> p (a t) n")
                if r:
                    dve.tensor_tensor(gate[:], ps_acc[:, 1], gate[:], ALU.mult).then_inc(gate_used, 1)
                    dve.wait_ge(gate_used, cc * 2 + CH + 1 + FREE)
                    dve.tensor_tensor(part, part, gate[:], ALU.add).then_inc(gate_used, 1)
                else:
                    dve.tensor_tensor(part, ps_acc[:, 1], gate[:], ALU.mult).then_inc(gate_used, 1)

            def res_sum(cc, v):
                dve.wait_ge(res_landed[v % LAND], cc * 64 + (v // LAND + 1) * 16)
                for k in range(2):
                    t = 2 * v + k
                    src = res_land[:, v % LAND, k]
                    if t == 0:
                        if not isinstance(cc, int) or cc > 0:
                            dve.wait_ge(rsum, cc)
                            dve.wait_ge(rg_rdy, cc + FREE)
                        ins = dve.tensor_scalar(racc[:], src, cvec[:, 0:1], None, ALU.mult)
                    else:
                        st.sync()
                        ins = dve.scalar_tensor_tensor(racc[:], src, cvec[:, t:t + 1], racc[:], ALU.mult,
                                                       ALU.add)
                    if k == 0:
                        st.did(ins)
                    else:
                        st.did(ins, res_used, cc * 16 + v + 1 + LAND)

            def merge(cc, r, prev):
                n0 = (N_MR0 if r else N_MA0) + cc * (GU + RU)
                for u in range(GU + RU):
                    lo(n0, u)
                    if u == 1:
                        prev()
                    if u == GU + 1:
                        gate_add(cc, r)
                    if not r:
                        for i in range(2):
                            rg_step(u - BLK_AT(i), cc * 2 + i)
                    else:
                        if 2 <= u < 22 and (u - 2) % 5 != 4:
                            res_sum(cc, u - 2 - (u - 2) // 5)
                        if u == 23:
                            dve.wait_ge(rsum, cc + 1)
                            dve.wait_ge(rbias_in, cc * 16 + 16)
                            dve.tensor_tensor(res_gate[:, ds(cc, 1)].rearrange("p a n -> p (a n)"),
                                              ps_c[:], rbias[:], ALU.add).then_inc(rg_rdy, 1)

            def merge_prev(cc, r):
                merge_in(cc, r)

            per = []

            def counted(f):
                n = st.n
                f()
                per.append(st.n - n)

            counted(lambda: merge(0, 0, lambda: zr_mul(3, 1)))
            b0, p0 = st.n, per[-1]
            with dve.Fori(1, CH) as cc:
                st.n, st.base = 0, (cc - 1) * p0 + b0
                merge(cc, 0, lambda: merge_prev(cc - 1, 0))
                assert st.n == p0
            st.n, st.base, st.last = b0 + (CH - 1) * p0, 0, None
            st.last = (dve_step, st.n)
            counted(lambda: merge(0, 1, lambda: merge_prev(CH - 1, 0)))
            b1, p1 = st.n, per[-1]
            with dve.Fori(1, CH - 1) as cc:
                st.n, st.base = 0, (cc - 1) * p1 + b1
                merge(cc, 1, lambda: merge_prev(cc - 1, 1))
                assert st.n == p1
            st.n, st.base = b1 + (CH - 2) * p1, 0
            st.last = (dve_step, st.n)

            def mt_lo(k):
                dve.wait_ge(mt_h, k + 1)
                dve.tensor_tensor(h_lo[:, k * BPJ:(k + 1) * BPJ], mt_ps(k),
                                  h_hi[:, k * BPJ:(k + 1) * BPJ].bitcast(F32), ALU.subtract).then_inc(mt_rdy, 1)

            cc = CH - 1
            n0 = N_MR0 + cc * (GU + RU)
            for u in range(GU + RU):
                lo(n0, u)
                if u == 1:
                    merge_prev(cc - 1, 1)
                if u == GU + 1:
                    gate_add(cc, 1)
                if 2 <= u < 22 and (u - 2) % 5 != 4:
                    res_sum(cc, u - 2 - (u - 2) // 5)
                if u >= GU + 2:
                    mt_lo(u - GU - 2)
                if u == 23:
                    dve.wait_ge(rsum, cc + 1)
                    dve.wait_ge(rbias_in, cc * 16 + 16)
                    dve.tensor_tensor(res_gate[:, cc], ps_c[:], rbias[:], ALU.add).then_inc(rg_rdy, 1)

            def out_sum(cc, par):
                dve.wait_ge(unit_done, N_OUT0 + (cc + 1) * GU + PARTS)
                dve.wait_ge(xo_in[par], (cc - par) * 8 + 16)
                if not isinstance(cc, int) or cc > 0:
                    dve.wait_ge(out_rdy, cc)
                else:
                    dve.wait_ge(rg_rdy, CH + FREE)
                dve.tensor_tensor(otmp[:], ps_acc[:, par], res_gate[:, ds(cc, 1)].rearrange("p a n -> p (a n)")
                                  .unsqueeze(1).to_broadcast([P, NT, CW]), ALU.mult).then_inc(acc_free, 1)
                dve.wait_ge(acc_free, J_MA0 + cc + 1 + ACCS)
                dve.tensor_tensor(x_out[:, par], x_out[:, par], otmp[:], ALU.add).then_inc(out_rdy, 1)

            def out_jobs(cc, first):
                for u in range(2 * GU):
                    lo(N_OUT0 + cc * GU, u)
                    if u == 1:
                        if first:
                            merge_prev(CH - 1, 1)
                        else:
                            out_sum(cc - 1, 1)
                    if first and u == 0:
                        mt_lo(CH - 2)
                    if first and u == 5:
                        mt_lo(CH - 1)
                    if u == GU + 1:
                        out_sum(cc, 0)

            out_jobs(0, True)
            with dve.Fori(1, CH // 2) as pair:
                cc = pair * 2
                out_jobs(cc, False)
            out_sum(CH - 1, 1)

        @block.tensor
        def _(pe):
            def unit(n0, u, left_hi, left_lo, par, first, last, acc_at=None):
                if first:
                    for what, count in acc_at:
                        pe.wait_ge(what, count)
                pe.wait_ge(hi_rdy, n0 + u + 1)
                for kk in range(UK):
                    for t in range(NT):
                        out = ps_acc[:, par, t]
                        pe.matmul(out, left_hi(kk, t), w_hi[:, u % PARTS, kk], start=first and kk == 0,
                                  stop=False)
                        ins = pe.matmul(out, left_lo(kk, t), w_hi[:, u % PARTS, kk], start=False, stop=False)
                ins.then_inc(hi_used, 1)
                pe.wait_ge(split_done, n0 + u + 1 + LAND)
                for kk in range(UK):
                    for t in range(NT):
                        ins = pe.matmul(ps_acc[:, par, t], left_hi(kk, t), w_lo[:, u % PARTS, kk],
                                        start=False, stop=last and kk == UK - 1)
                ins.then_inc(unit_done, 1)

            def rows_of(hi_, lo_, k0):
                return (lambda kk, t: hi_[:, k0 + kk, t]), (lambda kk, t: lo_[:, k0 + kk, t])

            def prep_turn(hg):
                pe.wait_ge(xs_rdy, hg * 2 + 2)
                pe.wait_ge(h_mod, hg * 4)
                for kk in range(BPJ):
                    for t in range(NT):
                        ins = pe.transpose(ps_t[:, kk // 2, kk % 2, t], xs[:, t, kk * P:(kk + 1) * P], ident[:])
                ins.then_inc(xs_t, 1)

            def prep_sum(hg):
                pe.wait_ge(ada_used, hg * 32 + 32 + LAND)
                pe.wait_ge(mod_rdy, hg)
                for s in range(2):
                    for kk in range(BPJ):
                        ins = pe.matmul(ps_c[:, s * BPJ + kk:s * BPJ + kk + 1], acc[:, s, kk * P:(kk + 1) * P],
                                        ones[:, 0:1], start=True, stop=True)
                ins.then_inc(colsum, 1)

            pe.wait_ge(consts, 5)
            pe.wait_ge(small_in, 176)
            pe.transpose(bank4[:, 0:98], raw1[0:98, :], ident[0:98, 0:98]).then_inc(cols_t, 1)
            pe.transpose(bank5[:, 0:P], raw2[:], ident[:]).then_inc(cols_t, 1)
            for hg in range(2):
                if hg == 0:
                    pe.wait_ge(sp_in, 1)
                prep_turn(hg)
                prep_sum(hg)

            def f_product():
                pe.wait_ge(wf_rdy, 1)
                for k in range(KT):
                    w = [wf_parts[:, k, s].rearrange("p a h -> p (a h)") for s in range(2)]
                    h_parts = [x[:, k].rearrange("p t n -> p (t n)") for x in (h_hi, h_lo)]
                    pe.matmul(bank4[0:48, 0:SEQ], w[0], h_parts[0], start=k == 0, stop=False)
                    pe.matmul(bank4[0:48, 0:SEQ], w[0], h_parts[1], start=False, stop=False)
                    ins = pe.matmul(bank4[0:48, 0:SEQ], w[1], h_parts[0], start=False, stop=k == KT - 1)
                ins.then_inc(f_done, 1)

            def wave_body(g, b, ada):
                n0 = b * BODY + g * 2 * BODY
                j0 = b * JPB + g * 2 * JPB
                hg = b + 2 * g + 2
                for i in range(JPB):
                    for u in range(WU):
                        lh, ll = rows_of(h_hi, h_lo, (g * WU + u) * UK)
                        if (i, u) == (0, WU // 2):
                            pe.wait_ge(h_rdy, 2 * g + 2)
                        unit(n0, i * WU + u, lh, ll, i % 2, u == 0, u == WU - 1,
                             ((acc_free, j0 + i + 1),))
                        if ada and (i, u) == (5, 0):
                            prep_turn(hg)
                        if ada and (i, u) == (9, 0):
                            prep_sum(hg)
                        if not ada and isinstance(b, int) and b == 0:
                            if (i, u) == (4, 0):
                                f_product()

            for g in range(WAVES):
                pe.wait_ge(h_rdy, 2 * g + 1)
                if g < WAVES - 1:
                    with pe.Fori(0, HALVES) as b:
                        wave_body(g, b, True)
                else:
                    wave_body(g, 0, False)
                    wave_body(g, 1, False)

            def head_step(step, h):
                if step == "turn":
                    pe.wait_ge(qn_rdy, h * 2 + 2)
                    pe.wait_ge(qkt_rdy, h * 2)
                    for s in range(2):
                        for t in range(NT):
                            ins = pe.transpose(tq[:, s * 2 + t], qn[:, s, t], ident[:])
                    ins.then_inc(turned, 1)
                if step == "score":
                    pe.wait_ge(lr_rdy, h * 2 + 2)
                    pe.wait_ge(qkt_rdy, h * 2 + 2)
                    pe.wait_ge(pr_rdy, h * 2)
                    for t in range(NT):
                        out = bank5[:, t * P:t * P + (t + 1) * P]
                        pe.matmul(out, fl[:, t * P:(t + 1) * P], fr[:, 0:(t + 1) * P], start=True, stop=False)
                        ins = pe.matmul(out, qkt[:, 0, t * P:(t + 1) * P], qkt[:, 1, 0:(t + 1) * P],
                                        start=False, stop=True)
                    ins.then_inc(scored, 1)
                if step == "probs":
                    pe.wait_ge(pr_rdy, h * 2 + 2)
                    pe.wait_ge(prt_rdy, h)
                    for k in range(3):
                        ins = pe.transpose(ps_p[:, k], pr[:, k], ident[:])
                    ins.then_inc(pr_t, 1)
                if step == "value":
                    pe.wait_ge(prt_rdy, h + 1)
                    pe.wait_ge(ya_rdy, h)
                    v = lambda s: store[:, ds(V_BLK + h, 1), s].rearrange("p a d -> p (a d)")
                    pe.matmul(ps_o[:, 0], prt[:, 0], v(0), start=True, stop=True)
                    pe.matmul(ps_o[:, 1], prt[:, 1], v(0), start=True, stop=False)
                    pe.matmul(ps_o[:, 1], prt[:, 2], v(1), start=False, stop=True).then_inc(valued, 1)
                if step == "y":
                    pe.wait_ge(y_rdy, h * 2 + 2)
                    for t in range(NT):
                        ins = pe.transpose(ps_y[:, t], yt[:, t], ident[:])
                    ins.then_inc(y_t, 1)

            def heads_body(it, first):
                n0 = N_HEADS0 + it * 2 * GU
                for u in range(2 * GU):
                    k = u % GU
                    lh, ll = rows_of(h_hi, h_lo, k * UK)
                    unit(n0, u, lh, ll, u // GU, k == 0, k == GU - 1, 
                         ((acc_free, J_HEADS0 + it * 2 + u // GU + 1),))
                    for step, i in heads_at.get(u, []):
                        head_step(step, it * 8 + i)

            heads_body(0, True)
            heads_body(1, False)

            def merge(cc, r, last=False):
                n0 = (N_MR0 if r else N_MA0) + cc * (GU + RU)
                b_hi, b_lo = (yr_hi, yr_lo) if r else (ya_hi, ya_lo)
                for u in range(GU + RU):
                    if u < GU:
                        lh, ll = rows_of(h_hi, h_lo, u * UK)
                        unit(n0, u, lh, ll, 0, u == 0, u == GU - 1,
                             ((acc_free, J_MA0 + 1), (gate_sum, cc + r * CH + FREE)))
                    else:
                        if u == GU:
                            pe.wait_ge(*((yr_rdy, BLOCKS) if r else (ya_rdy, HEADS)))
                        lh, ll = rows_of(b_hi, b_lo, (u - GU) * UK)
                        unit(n0, u, lh, ll, 1, u == GU, u == GU + RU - 1,
                             ((acc_free, J_MA0 + 2), (gate_used, (CH + 2 * cc if r else cc) + FREE)))
                    for i in range(2):
                        n = cc * 2 + i
                        if not r and u == BLK_AT(i):
                            pe.wait_ge(xz_rdy, n + 1)
                            pe.wait_ge(hh_rdy, n + FREE)
                            for s in range(2):
                                for t in range(NT):
                                    ins = pe.transpose(rt[:, s * 2 + t], xz[:, s, t], ident[:])
                            ins.then_inc(xz_t, 1)
                        if not r and u == BLK_AT(i) + 3:
                            pe.wait_ge(xc_rdy, n + 1)
                            pe.wait_ge(wrg_in, n * 32 + 32)
                            pe.wait_ge(ri_rdy, n * 4 + FREE)
                            for s in range(2):
                                ins = pe.matmul(ps_g[:, s], wrg[:, s], xc[:], start=True, stop=True)
                            ins.then_inc(rg_done, 1)
                    if r and u == 22:
                        pe.wait_ge(res_used, cc * 16 + 16 + LAND)
                        pe.wait_ge(rg_rdy, cc + FREE)
                        pe.matmul(ps_c[:], ones[:], racc[:], start=True, stop=True).then_inc(rsum, 1)
                    if last and GU <= u < GU + CH - 1:
                        mt_turn(u - GU)

            def mt_turn(k):
                pe.wait_ge(mt_rdy, k)
                pe.wait_ge(gate_used, CH + 2 * k + 2 + FREE)
                for kk in range(BPJ):
                    for t in range(NT):
                        ins = pe.transpose(ps_t[:, kk // 2, kk % 2, t], merged[:, k, t, kk * P:(kk + 1) * P],
                                           ident[:])
                ins.then_inc(mt_t, 1)

            with pe.Fori(0, CH) as cc:
                merge(cc, 0)
            with pe.Fori(0, CH - 1) as cc:
                merge(cc, 1)
            merge(CH - 1, 1, True)

            def out_jobs(cc, first):
                for u in range(2 * GU):
                    k = u % GU
                    if first and u < GU and k % 2 == 0:
                        pe.wait_ge(mt_rdy, k // 2 + 1)
                    lh, ll = rows_of(h_hi, h_lo, k * UK)
                    before = ((gate_sum, 2 * CH + FREE), (gate_used, 3 * CH + FREE))[u // GU]
                    unit(N_OUT0 + cc * GU, u, lh, ll, u // GU, k == 0, k == GU - 1,
                         (before if first else (acc_free, J_MA0 + ACCS + cc + u // GU - 1),))
                    if first and u == 3:
                        mt_turn(CH - 1)

            out_jobs(0, True)
            with pe.Fori(1, CH // 2) as pair:
                cc = pair * 2
                out_jobs(cc, False)


_INS = ["x", "c", "w_ada", "b_ada", "norm_w", "w_in", "b_f", "q_norm_w", "k_norm_w", "conv_w", "conv_b",
        "w_rg_a", "b_rg_a", "w_rg_x", "b_rg_x", "lru_lambda", "w_br_attn", "w_br_rnn", "w_gate", "b_gate",
        "w_out"]


def kernel(**inputs):
    import numpy as np
    import concourse.bacc as bacc
    from concourse.bass_utils import run_bass_kernel_spmd

    nc = bacc.Bacc("TRN2", target_bir_lowering=False, num_devices=1)
    arrays, args = {}, []
    for name in _INS:
        a = np.ascontiguousarray(inputs[name])
        arrays[f"in_{name}"] = a
        args.append(nc.dram_tensor(f"in_{name}", a.shape, mybir.dt.from_np(a.dtype), kind="ExternalInput").ap())
    out = nc.dram_tensor("out_y", (1, SEQ, D), F32, kind="ExternalOutput").ap()
    build(nc, *args, out)
    r = run_bass_kernel_spmd(nc, [arrays], core_ids=[0])
    return r.results[0]["out_y"]
```
